# Optimizing a Trainium2 kernel written in Bass

```python
import jax, jax.numpy as jnp
from jax import lax
import numpy as np

D_MODEL = 1024
BATCH = 1
SEQ = 1024
DEPTH = 1

D_MIX = D_MODEL
N_BRANCH = 3
LRU_HEADS = 4
LRU_BLOCK = D_MIX // LRU_HEADS
LRU_CONV_WIDTH = 4
LRU_C = 8.0
HGRN_HEADS = 8
HGRN_DK = D_MIX // HGRN_HEADS
HGRN_DV = D_MIX // HGRN_HEADS
HGRN_CHUNK = 64
GATE_CLIP = 30.0
CONF_WIDTH = 31
MEM_LEN = 256
XA_HEADS = 4
XA_HEAD_DIM = D_MODEL // XA_HEADS
D_FF = 4 * D_MODEL
EPS = 1e-6
IN_SPLIT_SIZES = (D_MIX, D_MIX,
                  D_MIX, D_MIX, D_MIX, D_MIX,
                  D_MIX, D_MIX,
                  N_BRANCH * D_MODEL)
N_IN = sum(IN_SPLIT_SIZES)

kernel_name = "hybrid_rglru_hgrn2_conformer_block"

def rmsnorm(x, g):
    xf = x.astype(jnp.float32)
    y = xf * lax.rsqrt(jnp.mean(xf * xf, axis=-1, keepdims=True) + EPS)
    return (y * g.astype(jnp.float32)).astype(x.dtype)

def layernorm(x, g, b):
    xf = x.astype(jnp.float32)
    mu = jnp.mean(xf, axis=-1, keepdims=True)
    xc = xf - mu
    var = jnp.mean(xc * xc, axis=-1, keepdims=True)
    y = xc * lax.rsqrt(var + EPS) * g.astype(jnp.float32) + b.astype(jnp.float32)
    return y.astype(x.dtype)

def causal_dw_conv(x, w, b):
    k, c = w.shape
    y = lax.conv_general_dilated(
        x, w[:, None, :].astype(x.dtype), window_strides=(1,),
        padding=((k - 1, 0),), dimension_numbers=("NWC", "WIO", "NWC"),
        feature_group_count=c)
    return y + b.astype(x.dtype)

def _lin_combine(left, right):
    a_l, b_l = left
    a_r, b_r = right
    return a_l * a_r, a_r * b_l + b_r

def rglru_branch(xb, yb, conv_w, conv_b, wx, bx, wa, ba, lam):
    bsz, s, _ = xb.shape
    xc = causal_dw_conv(xb, conv_w, conv_b)
    xh = xc.reshape(bsz, s, LRU_HEADS, LRU_BLOCK)
    gate_x = jax.nn.sigmoid(jnp.einsum("bshi,hij->bshj", xh, wx).reshape(bsz, s, D_MIX) + bx)
    gate_a = jax.nn.sigmoid(jnp.einsum("bshi,hij->bshj", xh, wa).reshape(bsz, s, D_MIX) + ba)
    log_a = -LRU_C * gate_a.astype(jnp.float32) * jax.nn.softplus(-lam.astype(jnp.float32))
    log_a = jnp.minimum(log_a, -1e-6)
    a = jnp.exp(log_a)
    mult = jnp.sqrt(-jnp.expm1(2.0 * log_a))
    u = xc.astype(jnp.float32) * gate_x.astype(jnp.float32) * mult
    _, h = lax.associative_scan(_lin_combine, (a, u), axis=1)
    return h.astype(xb.dtype) * jax.nn.gelu(yb)

def hgrn2_branch(q, f, i, g, lb, norm_g):
    bsz, s, _ = q.shape
    dtype = q.dtype
    n_chunks = s // HGRN_CHUNK
    lb = lb.astype(jnp.float32)
    qf = jax.nn.silu(q.astype(jnp.float32)) * (HGRN_DK ** -0.5)
    z = jnp.clip(f.astype(jnp.float32), -GATE_CLIP, GATE_CLIP)
    logf = jax.nn.log_sigmoid(z) + jnp.log1p(lb * jnp.exp(-z))
    logf = jnp.minimum(logf, 0.0)
    kf = -jnp.expm1(logf)
    vf = i.astype(jnp.float32)

    def to_chunks(t):
        return t.reshape(bsz, n_chunks, HGRN_CHUNK, HGRN_HEADS, -1).transpose(1, 0, 3, 2, 4)

    causal = jnp.tril(jnp.ones((HGRN_CHUNK, HGRN_CHUNK), dtype=bool))[:, :, None]

    def step(state, inp):
        qc, kc, vc, gc = inp
        bcum = jnp.cumsum(gc, axis=2)
        o_inter = jnp.einsum("bhcd,bhde->bhce", qc * jnp.exp(bcum), state)
        diff = bcum[:, :, :, None, :] - bcum[:, :, None, :, :]
        decay = jnp.where(causal, jnp.exp(jnp.where(causal, diff, 0.0)), 0.0)
        attn = jnp.einsum("bhid,bhijd,bhjd->bhij", qc, decay, kc)
        o = o_inter + jnp.einsum("bhij,bhje->bhie", attn, vc)
        b_last = bcum[:, :, -1:, :]
        state = (jnp.exp(b_last[:, :, 0, :])[..., None] * state
                 + jnp.einsum("bhcd,bhce->bhde", kc * jnp.exp(b_last - bcum), vc))
        return state, o

    s0 = jnp.zeros((bsz, HGRN_HEADS, HGRN_DK, HGRN_DV), jnp.float32)
    _, o = lax.scan(step, s0, (to_chunks(qf), to_chunks(kf), to_chunks(vf), to_chunks(logf)))
    o = o.transpose(1, 0, 3, 2, 4).reshape(bsz, s, HGRN_HEADS, HGRN_DV)
    gg = jax.nn.silu(g.astype(jnp.float32)).reshape(bsz, s, HGRN_HEADS, HGRN_DV)
    o = rmsnorm(o, norm_g) * gg
    return o.reshape(bsz, s, D_MIX).astype(dtype)

def conformer_conv_branch(va, vg, dw_w, dw_b, ln_g, ln_b):
    u = va * jax.nn.sigmoid(vg)
    u = causal_dw_conv(u, dw_w, dw_b)
    u = layernorm(u, ln_g, ln_b)
    return jax.nn.silu(u)

def cross_attention(h, mem_n, wq, wkv, wo):
    bsz, s, _ = h.shape
    m = mem_n.shape[1]
    q = (h @ wq).reshape(bsz, s, XA_HEADS, XA_HEAD_DIM)
    k, v = jnp.split(mem_n @ wkv, 2, axis=-1)
    k = k.reshape(bsz, m, XA_HEADS, XA_HEAD_DIM)
    v = v.reshape(bsz, m, XA_HEADS, XA_HEAD_DIM)
    sc = jnp.einsum("bshd,bmhd->bhsm", q, k).astype(jnp.float32) * (XA_HEAD_DIM ** -0.5)
    p = jax.nn.softmax(sc, axis=-1).astype(h.dtype)
    o = jnp.einsum("bhsm,bmhd->bshd", p, v).reshape(bsz, s, D_MODEL)
    return o @ wo

def setup_inputs(seed: int = 0) -> dict:
    key = jax.random.key(seed)
    ks = iter(jax.random.split(key, 40))
    L = DEPTH

    def nrm(shape, scale):
        return jax.random.normal(next(ks), shape, jnp.float32) * scale

    def gain(shape):
        return 1.0 + nrm(shape, 0.02)

    x = nrm((BATCH, SEQ, D_MODEL), 1.0)
    mem = nrm((BATCH, MEM_LEN, D_MODEL), 1.0)
    hgrn_lower_bounds = nrm((L, D_MIX), 1.0)
    norm_pre_mix = gain((L, D_MODEL))
    norm_post_mix = gain((L, D_MODEL))
    w_in = nrm((L, D_MODEL, N_IN), D_MODEL ** -0.5)
    lru_conv_w = nrm((L, LRU_CONV_WIDTH, D_MIX), LRU_CONV_WIDTH ** -0.5)
    lru_conv_b = nrm((L, D_MIX), 0.01)
    lru_wx = nrm((L, LRU_HEADS, LRU_BLOCK, LRU_BLOCK), LRU_BLOCK ** -0.5)
    lru_bx = nrm((L, D_MIX), 0.01)
    lru_wa = nrm((L, LRU_HEADS, LRU_BLOCK, LRU_BLOCK), LRU_BLOCK ** -0.5)
    lru_ba = nrm((L, D_MIX), 0.01)
    u = jax.random.uniform(next(ks), (L, D_MIX), jnp.float32, 0.9, 0.999)
    a0 = u ** (1.0 / LRU_C)
    lru_lambda = jnp.log(a0) - jnp.log1p(-a0)
    hgrn_norm_g = gain((L, HGRN_DV))
    conf_dw_w = nrm((L, CONF_WIDTH, D_MIX), CONF_WIDTH ** -0.5)
    conf_dw_b = nrm((L, D_MIX), 0.01)
    conf_ln_g = gain((L, D_MIX))
    conf_ln_b = nrm((L, D_MIX), 0.01)
    w_branch = nrm((L, N_BRANCH, D_MIX, D_MODEL), D_MIX ** -0.5)
    w_mix_out = nrm((L, D_MODEL, D_MODEL), D_MODEL ** -0.5)
    norm_pre_xa = gain((L, D_MODEL))
    norm_post_xa = gain((L, D_MODEL))
    mem_norm_g = gain((L, D_MODEL))
    xa_wq = nrm((L, D_MODEL, D_MODEL), D_MODEL ** -0.5)
    xa_wkv = nrm((L, D_MODEL, 2 * D_MODEL), D_MODEL ** -0.5)
    xa_wo = nrm((L, D_MODEL, D_MODEL), D_MODEL ** -0.5)
    norm_pre_mlp = gain((L, D_MODEL))
    norm_post_mlp = gain((L, D_MODEL))
    mlp_w1 = nrm((L, D_MODEL, D_FF), D_MODEL ** -0.5)
    mlp_w2 = nrm((L, D_FF, D_MODEL), D_FF ** -0.5)
    return {"x": x, "mem": mem, "hgrn_lower_bounds": hgrn_lower_bounds,
            "norm_pre_mix": norm_pre_mix, "norm_post_mix": norm_post_mix, "w_in": w_in,
            "lru_conv_w": lru_conv_w, "lru_conv_b": lru_conv_b, "lru_wx": lru_wx,
            "lru_bx": lru_bx, "lru_wa": lru_wa, "lru_ba": lru_ba, "lru_lambda": lru_lambda,
            "hgrn_norm_g": hgrn_norm_g, "conf_dw_w": conf_dw_w, "conf_dw_b": conf_dw_b,
            "conf_ln_g": conf_ln_g, "conf_ln_b": conf_ln_b, "w_branch": w_branch,
            "w_mix_out": w_mix_out, "norm_pre_xa": norm_pre_xa, "norm_post_xa": norm_post_xa,
            "mem_norm_g": mem_norm_g, "xa_wq": xa_wq, "xa_wkv": xa_wkv, "xa_wo": xa_wo,
            "norm_pre_mlp": norm_pre_mlp, "norm_post_mlp": norm_post_mlp,
            "mlp_w1": mlp_w1, "mlp_w2": mlp_w2}

def reference(x, mem, hgrn_lower_bounds, norm_pre_mix, norm_post_mix, w_in,
              lru_conv_w, lru_conv_b, lru_wx, lru_bx, lru_wa, lru_ba, lru_lambda,
              hgrn_norm_g, conf_dw_w, conf_dw_b, conf_ln_g, conf_ln_b, w_branch,
              w_mix_out, norm_pre_xa, norm_post_xa, mem_norm_g, xa_wq, xa_wkv, xa_wo,
              norm_pre_mlp, norm_post_mlp, mlp_w1, mlp_w2):
    bsz, s, _ = x.shape
    lb_soft = jax.nn.softmax(hgrn_lower_bounds.astype(jnp.float32), axis=0)
    lb_all = jnp.cumsum(lb_soft, axis=0) - lb_soft[0]
    split_idx = list(np.cumsum(IN_SPLIT_SIZES)[:-1])

    for l in range(DEPTH):
        h = rmsnorm(x, norm_pre_mix[l])
        z = h @ w_in[l]
        lru_x, lru_y, hq, hf, hi, hg, ca, cg, gate_logits = jnp.split(z, split_idx, axis=-1)
        y_lru = rglru_branch(lru_x, lru_y, lru_conv_w[l], lru_conv_b[l], lru_wx[l], lru_bx[l],
                             lru_wa[l], lru_ba[l], lru_lambda[l])
        y_hgrn = hgrn2_branch(hq, hf, hi, hg, lb_all[l], hgrn_norm_g[l])
        y_conf = conformer_conv_branch(ca, cg, conf_dw_w[l], conf_dw_b[l], conf_ln_g[l], conf_ln_b[l])
        branches = jnp.stack([y_lru, y_hgrn, y_conf], axis=2)
        proj = jnp.einsum("bsnw,nwd->bsnd", branches, w_branch[l])
        gates = jax.nn.sigmoid(gate_logits.reshape(bsz, s, N_BRANCH, D_MODEL))
        mixed = jnp.sum(gates * proj, axis=2) @ w_mix_out[l]
        x = x + rmsnorm(mixed, norm_post_mix[l])
        h = rmsnorm(x, norm_pre_xa[l])
        mem_n = rmsnorm(mem, mem_norm_g[l])
        xa = cross_attention(h, mem_n, xa_wq[l], xa_wkv[l], xa_wo[l])
        x = x + rmsnorm(xa, norm_post_xa[l])
        h = rmsnorm(x, norm_pre_mlp[l])
        ff = jnp.square(jax.nn.relu(h @ mlp_w1[l])) @ mlp_w2[l]
        x = x + rmsnorm(ff, norm_post_mlp[l])
    return x


_drawn_inputs = setup_inputs


def setup_inputs(seed=0):
    import zlib

    import numpy as np

    out = dict(_drawn_inputs(seed))
    spreads = {}
    factors = {'norm_pre_mix': 2.94,
     'norm_post_mix': 3.87,
     'lru_bx': 24.672,
     'lru_ba': 32.12,
     'hgrn_norm_g': 5.748,
     'conf_dw_b': 6.065,
     'conf_ln_g': 15.961,
     'conf_ln_b': 30.1,
     'norm_pre_xa': 4.797,
     'norm_post_xa': 15.448,
     'mem_norm_g': 3.139,
     'norm_pre_mlp': 46.393,
     'norm_post_mlp': 97.627}
    for name, (base, spread) in spreads.items():
        noise = np.random.default_rng([zlib.crc32(name.encode()), seed]).standard_normal(out[name].shape)
        drawn = base * np.exp(spread * noise) if base else spread * noise
        out[name] = __import__('jax').numpy.asarray(drawn.astype(out[name].dtype))
    for name, factor in factors.items():
        out[name] = (out[name] * factor).astype(out[name].dtype)
    return out
```

```python
from contextlib import ExitStack

import concourse.bass as bass
from concourse import mybir

F32 = mybir.dt.float32
F32R = mybir.dt.float32r
U8 = mybir.dt.uint8
ACT = mybir.ActivationFunctionType
ALU = mybir.AluOpType
AX_X = mybir.AxisListType.X

P = 128
D = 1024
T = 1024
M = 256
KB = D // P
HALF = T // 2
CHUNK = 128
NCH = T // CHUNK
LEVELS = 7
CW, LW = 31, 4
FFB = 4
EPS = 1e-6
CLIP = 30.0
LRU_C = 8.0
DK_SCALE = float(P) ** -0.5
XA_HEADS = 4
XA_SCALE = float(D // XA_HEADS) ** -0.5
MT = M // P
ST = HALF // P

(G_PRE_MIX, G_POST_MIX, G_PRE_XA, G_POST_XA, G_PRE_MLP, G_POST_MLP, G_MEM, HLB, LRU_B, LRU_BX,
 LRU_BA, LRU_LAM, HG_G, CONF_B, CONF_G, CONF_LB) = range(16)
LRU_W = 16
CONF_W = LRU_W + LW
NP = CONF_W + CW

NEG = 10
NEG_GAINS = (G_MEM, G_PRE_MIX, G_PRE_XA, G_PRE_MLP)

N_KV = 0
N_CONF = N_KV + 2 * KB
N_LRU = N_CONF + 2 * KB
N_HG = N_LRU + 2 * KB
N_GATE = N_HG + 4 * KB
N_BR = N_GATE + 3 * KB
N_MIX = N_BR + 2 * 3 * KB
N_Q = N_MIX + 2 * KB
N_WO = N_Q + 2 * KB
N_MLP = N_WO + 2 * KB
N_END = N_MLP + 2 * 2 * FFB * KB
W_BR = N_BR
W_MIX = W_BR + 3 * KB
W_Q = W_MIX + KB
W_WO = W_Q + KB
W_MLP = W_WO + KB
W_END = W_MLP + 2 * FFB * KB
MLP_ORDER = [("up", 0), ("up", 1), ("down", 0), ("up", 2), ("down", 1), ("up", 3), ("down", 2), ("down", 3)]


class Steps:

    def __init__(self, eng, sem):
        self.eng, self.sem, self.base, self.k = eng, sem, 0, 0

    def at(self, ins):
        ins.then_inc(self.sem, 1)
        self.k += 1
        return self.base + self.k

    def wait(self, value):
        self.eng.wait_ge(self.sem, value)

    def loop(self, per, start=0):
        self.per, self.start, self.before = per, start, self.base + self.k

    def body(self, i):
        self.base, self.k = self.before + (i - self.start) * self.per, 0

    def end(self, n):
        assert self.k == self.per, (self.k, self.per)
        self.base, self.k = self.before + (n - self.start) * self.per, 0


def runs(eng, n, peel=1):
    yield from range(peel)
    with eng.Fori(peel, n) as i:
        yield i


def first(i):
    return type(i) is int and i == 0


def build(nc, xT, memT, wall, lru_gates, params, masks, ident_in, out):
    with ExitStack() as ctx:
        def sem(name):
            return ctx.enter_context(nc.semaphore(name))

        def sems(name, n=2):
            return [sem(f"{name}{i}") for i in range(n)]

        origin = -(-nc.sbuf_base // 64) * 64

        def at(name, offset, shape, dt=F32):
            return nc.alloc_sbuf_tensor_at(name, shape, dt, offset=origin + offset)

        ROW = T * 4
        HROW = HALF * 4
        ident = at("ident", 0, [P, P])
        ones = at("ones", 512, [P, P])
        lvmask = at("lvmask", 1024, [P, LEVELS, CHUNK // 2], U8)
        par = at("par", 1472, [P, KB, NP])
        der = at("der", 1472 + 4 * KB * NP, [P, 16, KB])
        small = at("small", 1472 + 4 * KB * NP + 512, [P, 16])
        WGT = 1472 + 4 * KB * NP + 512 + 64
        w_raw = at("w_raw", WGT, [P, 2, KB, P])
        w_hi = at("w_hi", WGT + 2 * ROW, [P, 2, KB, P], F32R)
        w_lo = at("w_lo", WGT + 4 * ROW, [P, 2, KB, P], F32R)
        HT = WGT + 6 * ROW
        h_hi = at("h_hi", HT, [P, KB, T], F32R)
        h_lo = at("h_lo", HT + KB * ROW, [P, KB, T], F32R)
        xsq = at("xsq", HT + 14 * ROW, [P, 2, T])
        CONV = HT + 16 * ROW
        PAD = CW - 1
        UB = (T + PAD + 2) * 4
        ub = [at(f"ub{p}", CONV + p * UB, [P, T + PAD]) for p in range(2)]
        sigb = at("sigb", CONV + 2 * UB, [P, T])
        cacc = [at(f"cacc{p}", CONV + 2 * UB + (1 + p) * ROW, [P, T]) for p in range(2)]
        cout = at("cout", CONV + 2 * UB + 3 * ROW, [P, T])
        gbuf = at("gbuf", CONV + 2 * UB + 4 * ROW, [P, T])
        cmu = at("cmu", CONV + 2 * UB + 5 * ROW, [P, T])
        crs = at("crs", CONV + 2 * UB + 6 * ROW, [P, T])
        ARENA = CONV + 2 * UB + 7 * ROW
        kv_sb = [at(f"kv{i}", CONV + 2 * i * ROW, s, F32R) for i, s in
                 enumerate(([P, KB, M], [P, KB, M], [P, MT, D], [P, MT, D]))]
        macc = at("macc", CONV, [P, KB, HALF])
        gst = at("gst", CONV + 4 * ROW, [P, 2, HALF])
        assert 5 * ROW <= 2 * UB + 3 * ROW
        xx = [at(f"xx{h}", CONV + h * 4 * ROW, [P, KB, HALF]) for h in range(2)]
        sqm = at("sqm", ARENA - ROW, [P, 2, HALF])
        mask_f = at("mask_f", ARENA + 19 * ROW, [P, LEVELS, CHUNK // 2])
        x_sb = at("x_sb", ARENA, [P, KB, T])
        mem = at("mem", ARENA + 8 * ROW, [P, KB, M])
        mem_hi = at("mem_hi", ARENA + 10 * ROW, [P, KB, M], F32R)
        mem_lo = at("mem_lo", ARENA + 12 * ROW, [P, KB, M], F32R)
        mem_sq = at("mem_sq", ARENA + 14 * ROW, [P, KB, M])
        x_acc = at("x_acc", ARENA + 16 * ROW, [P, T])
        x_r = at("x_r", ARENA + 17 * ROW, [P, T])
        m_acc = at("m_acc", ARENA + 18 * ROW, [P, M])
        m_r = at("m_r", ARENA + 18 * ROW + 1024, [P, M])
        ht = at("ht", ARENA + 14 * ROW, [P, 2, T])
        LXB = (T + 2 * LW) * 4
        lxb = [at(f"lxb{p}", ARENA + p * LXB, [P, T + LW - 1]) for p in range(2)]
        L = ARENA + 2 * LXB
        lxc = at("lxc", L, [P, 2, T])
        lxc_hi = at("lxc_hi", L + 2 * ROW, [P, 2, T], F32R)
        lxc_lo = at("lxc_lo", L + 4 * ROW, [P, 2, T], F32R)
        ltanh = at("ltanh", L + 2 * ROW, [P, 2, T])
        ldec = at("ldec", L + 4 * ROW, [P, 2, T])
        lg_raw = at("lg_raw", L + 6 * ROW, [P, 2, 2, 2 * P])
        lg_hi = at("lg_hi", L + 7 * ROW, [P, 2, 2, 2 * P], F32R)
        lg_lo = at("lg_lo", L + 8 * ROW, [P, 2, 2, 2 * P], F32R)
        lgx = at("lgx", L + 9 * ROW, [P, 2, T])
        lga = at("lga", L + 11 * ROW, [P, 2, T])
        lsq = at("lsq", L + 13 * ROW, [P, 2, T])
        lgel = at("lgel", L + 15 * ROW, [P, 2, T])
        TOP = L + 17 * ROW
        assert origin + TOP <= nc.sbuf_usable_end, (origin + TOP, nc.sbuf_usable_end)
        names = ("zc", "sp", "sn", "f", "b", "k", "q", "qp2", "kp0", "kp1", "vt", "vtok", "gg", "attn",
                 "kr", "krt", "qpf", "state", "osq")
        hg = {}
        for i, name in enumerate(names):
            hg[name] = at(f"hg_{name}", ARENA + i * ROW, [P, T])
        hqp = [at(f"hg_qp{i}", ARENA + 7 * ROW + i * HROW, [P, HALF]) for i in range(2)]
        hg["qs"] = at("hg_qs", CONV, [P, T])
        hg["nw"] = at("hg_nw", CONV + ROW, [P, T])
        assert 2 * ROW <= 2 * UB
        hg["oc"] = at("hg_oc", CONV + 2 * UB + ROW, [P, T])
        hg["rt"] = at("hg_rt", CONV + 2 * UB + 2 * ROW, [P, T])
        yb_hi = [at(f"yb_hi{s}", ARENA + s * 8 * ROW, [P, KB, HALF], F32R) for s in range(2)]
        yb_lo = [at(f"yb_lo{s}", ARENA + s * 8 * ROW + 4 * ROW, [P, KB, HALF], F32R) for s in range(2)]
        yst = at("yst", ARENA + 16 * ROW, [P, 2, HALF])
        xs = at("xs", ARENA + 16 * ROW, [P, 2, HALF])
        nt = at("nt", ARENA + 17 * ROW, [P, 2, HALF])
        nacc = [at(f"nacc{h}", ARENA + 18 * ROW + h * HROW, [P, HALF]) for h in range(2)]
        rn = [at(f"rn{h}", ARENA + 19 * ROW + h * HROW, [P, HALF]) for h in range(2)]
        assert origin + ARENA + 20 * ROW <= nc.sbuf_usable_end, (origin + ARENA + 20 * ROW, nc.sbuf_usable_end)
        hx_hi = [at(f"hx_hi{h}", HT + h * 8 * ROW, [P, KB, HALF], F32R) for h in range(2)]
        hx_lo = [at(f"hx_lo{h}", HT + h * 8 * ROW + 4 * ROW, [P, KB, HALF], F32R) for h in range(2)]
        kh, kl = (at(f"k_{s}", HT + 2 * i * ROW, [P, KB, M], F32R) for i, s in enumerate(("hi", "lo")))
        vh, vl = (at(f"v_{s}", HT + (4 + 2 * i) * ROW, [P, MT, D], F32R) for i, s in enumerate(("hi", "lo")))
        prob = [at(f"prob{i}", HT + (8 + i) * ROW, [P, ST, M]) for i in range(2)]
        pt_hi = at("pt_hi", HT + 10 * ROW, [P, MT, HALF], F32R)
        pt_lo = at("pt_lo", HT + 11 * ROW, [P, MT, HALF], F32R)

        ps = [ctx.enter_context(nc.psum_tensor(f"ps{u}", [P, T], F32)) for u in range(2)]
        xa = ctx.enter_context(nc.psum_tensor("xa", [P, T], F32))
        xb = ctx.enter_context(nc.psum_tensor("xb", [P, T], F32))
        spare = [ps[u][:, HALF:] for u in range(2)]

        def dram(name, shape, dt=F32):
            return nc.dram_tensor(name, shape, dt, kind="Internal").ap()

        kv_d = [dram(f"kv_d{i}", [P, 2 * T]) for i in range(4)]
        glu_d = dram("glu_d", [KB // 2, P, T])
        conv_d = dram("conv_d", [KB, P, T])
        lru_d = dram("lru_d", [KB, P, T])
        hgrn_d = dram("hgrn_d", [KB, P, T])
        gate_d = dram("gate_d", [3 * KB, P, T])
        x_d = dram("x_d", [D, T])
        branch_d = (lru_d, hgrn_d, conv_d)

        def half_pair(d, t, h):
            return d[bass.ds(t, 2), :, h * HALF:(h + 1) * HALF].rearrange("t p n -> p t n")

        def rows_pair(d, j, h):
            return d[2 * j * P:(2 * j + 2) * P, h * HALF:(h + 1) * HALF].rearrange("(t p) n -> p t n", p=P)

        def pc(c, j):
            return par[:, bass.ds(c, 1), j]

        eps = small[:, 15:16]

        def one(d, t):
            return d[bass.ds(t, 1)].rearrange("t p n -> p (t n)")

        consts_in, mem_in = sem("consts_in"), sem("mem_in")
        x_in = sems("x_in")
        w_loaded = sems("w_loaded")
        w_split = sem("w_split")
        w_high = sem("w_high")
        mm_done = sem("mm_done")
        evac = sems("evac")
        dve_step, act_step = sem("dve_step"), sem("act_step")
        exps_ready = sem("exps_ready")
        consts_ready = sem("consts_ready")
        mem_sq_done, mem_acc_done, mem_stat, mem_rt = sem("mem_sq_done"), sem("mem_acc_done"), sem("mem_stat"), sem("mem_rt")
        mem_normed, mem_hi_done, mem_split = sem("mem_normed"), sem("mem_hi_done"), sem("mem_split")
        kv_hi_done, kv_stored = sem("kv_hi_done"), sem("kv_stored")
        xsq_done, xacc_done, x_stat, x_rt = sem("xsq_done"), sem("xacc_done"), sem("x_stat"), sem("x_rt")
        h_normed, h_hi_done, h_split = sem("h_normed"), sem("h_hi_done"), sem("h_split")
        conv_done, conv_stored, glu_stored, glu_loaded = sem("conv_done"), sem("conv_stored"), sem("glu_stored"), sem("glu_loaded")
        lg_loaded, lg_split, xc_ready, xc_hi_done, lru_split = (sem(s) for s in ("lg_loaded", "lg_split", "xc_ready", "xc_hi_done", "lru_split"))
        lmm_done, lgate_done, la_ready, ldec_done, lm_ready, lmult_done, ylru_ready = (
            sem(s) for s in ("lmm_done", "lgate_done", "la_ready", "ldec_done", "lm_ready", "lmult_done", "ylru_ready"))
        ylru_stored = sem("ylru_stored")
        hsig, hsigq, hsigg, diag_done, lv_ready, lv_done, lv_free = (
            sem(s) for s in ("hsig", "hsigq", "hsigg", "diag_done", "lv_ready", "lv_done", "lv_free"))
        vtr_done, vtok_done, kr_ready, ktr_done, krt_done, ds_done, state_ready = (
            sem(s) for s in ("vtr_done", "vtok_done", "kr_ready", "ktr_done", "krt_done", "ds_done", "state_ready"))
        out_done, osq_done, oc_done, hstat_done, hrt_done, hy_ready, hy_stored, hy_free = (
            sem(s) for s in ("out_done", "osq_done", "oc_done", "hstat_done", "hrt_done", "hy_ready", "hy_stored", "hy_free"))
        gate_stored = sems("gate_stored")
        csum_ready, cmean_mm, cmean_ready, cdev_loaded, cdev_ready, cdev_sq, cvar_ready, cvar_mm, cstd_ready = (
            sem(s) for s in ("csum_ready", "cmean_mm", "cmean_ready", "cdev_loaded", "cdev_ready", "cdev_sq",
                             "cvar_ready", "cvar_mm", "cstd_ready"))
        y_loaded, y_pre, y_hi_done, y_split = (sem(s) for s in ("y_loaded", "y_pre", "y_hi_done", "y_split"))
        g_loaded, g_used, mg_ready, mg_hi_done, mg_split = (sem(s) for s in ("g_loaded", "g_used", "mg_ready", "mg_hi_done", "mg_split"))
        sq_done = sem("sq_done")
        nacc_ready, nstat_done, nrt_done = sems("nacc_ready"), sems("nstat_done"), sems("nrt_done")
        xs_loaded, x_new, xnsq_done, xn_used, x_stored = (sem(s) for s in ("xs_loaded", "x_new", "xnsq_done", "xn_used", "x_stored"))
        hn_ready, hn_hi_done, hx_split = sem("hn_ready"), sem("hn_hi_done"), sem("hx_split")
        q_hi_done, kv_loaded = sem("q_hi_done"), sem("kv_loaded")
        sc_done, nmax_ready, exp_done, p_ready, tr_done, pt_hi_done, pt_split, pv_done, o_hi_done, o_split = (
            sem(s) for s in ("sc_done", "nmax_ready", "exp_done", "p_ready", "tr_done", "pt_hi_done", "pt_split",
                             "pv_done", "o_hi_done", "o_split"))
        relu_done, ff_hi_done, ff_split, ysq_done = (sem(s) for s in ("relu_done", "ff_hi_done", "ff_split", "ysq_done"))
        out_stored = sem("out_stored")

        block = ctx.enter_context(nc.Block())

        @block.tensor
        def _(pe):
            def mm3(out, wh, wl, xh, xl, start, stop):
                nc.tensor.matmul(out, wh, xh, start=start, stop=False)
                nc.tensor.matmul(out, wh, xl, start=False, stop=False)
                return nc.tensor.matmul(out, wl, xh, start=False, stop=stop)

            def take(m, u):
                pe.wait_ge(w_split, 2 * m + u + 1)
                if not first(m):
                    pe.wait_ge(evac[u], m)

            def product(u, out, hi, lo, cols=slice(None)):
                for k in range(KB):
                    mm = mm3(out, w_hi[:, u, k], w_lo[:, u, k], hi[:, k, cols], lo[:, k, cols], k == 0, k == KB - 1)
                return mm

            def half_of(u, n):
                cols = slice(n * HALF, (n + 1) * HALF)
                return product(u, ps[u][:, cols], h_hi, h_lo, cols)

            def full_tile(m, u):
                take(m, u)
                half_of(u, 0)
                half_of(u, 1).then_inc(mm_done, 1)

            def half_tiles(m0, m1, hi, lo):
                with pe.Fori(m0, m1) as m:
                    for u in range(2):
                        take(m, u)
                        product(u, ps[u][:, 0:HALF], hi, lo).then_inc(mm_done, 1)

            pe.wait_ge(consts_ready, 1)
            pe.wait_ge(mem_acc_done, 1)
            nc.tensor.matmul(xa[:, 0:M], ones[:], m_acc[:], start=True, stop=True).then_inc(mem_stat, 1)
            pe.wait_ge(mem_split, 1)
            for m in runs(pe, KB // 2):
                for u in range(2):
                    take(m, u)
                    product(u, ps[u][:, 0:M], mem_hi, mem_lo).then_inc(mm_done, 1)
            pe.wait_ge(xacc_done, KB)
            for n in range(2):
                cols = slice(n * HALF, (n + 1) * HALF)
                mm = nc.tensor.matmul(xb[:, cols], ones[:], x_acc[:, cols], start=True, stop=True)
            mm.then_inc(x_stat, 1)
            with pe.Fori(KB // 2, KB) as m:
                for u in range(2):
                    take(m, u)
                    for mt in range(MT):
                        cols = slice(mt * P, (mt + 1) * P)
                        for k in range(KB):
                            mm = mm3(ps[u][:, cols], mem_hi[:, k, cols], mem_lo[:, k, cols],
                                     w_hi[:, u, k], w_lo[:, u, k], k == 0, k == KB - 1)
                    mm.then_inc(mm_done, 1)

            pe.wait_ge(h_split, KB)
            with pe.Fori(N_CONF // 2, N_LRU // 2) as m:
                full_tile(m, 0)
                full_tile(m, 1)

            with pe.Fori(0, KB // 2) as b:
                m = N_LRU // 2 + 2 * b
                for q in range(4):
                    full_tile(m + q // 2, q % 2)
                pe.wait_ge(lg_split, b + 1)
                pe.wait_ge(lru_split, 2 * b + 2)
                for p in range(2):
                    for g, acc in enumerate((xa, xb)):
                        if p:
                            pe.wait_ge(lgate_done, 4 * b + g + 1)
                        for n in range(2):
                            cols = slice(n * HALF, (n + 1) * HALF)
                            for k in range(2):
                                w = slice(p * P, (p + 1) * P)
                                mm = mm3(acc[:, cols], lg_hi[:, g, k, w], lg_lo[:, g, k, w],
                                         lxc_hi[:, k, cols], lxc_lo[:, k, cols], k == 0, k == 1)
                        mm.then_inc(lmm_done, 1)

            def per_chunk(n, product):
                for c in range(n):
                    mm = product(c, slice(c * CHUNK, (c + 1) * CHUNK))
                return mm

            def level(h, l):
                pe.wait_ge(lv_ready, LEVELS * h + l)
                pe.wait_ge(lv_free, (LEVELS + 1) * h + max(l - 1, 1))
                keys = hg["k"] if l == 1 else hg[f"kp{l % 2}"]
                for c in range(NCH):
                    w = CHUNK // 2
                    at0 = (l % 2) * HALF + c * w
                    mm = nc.tensor.matmul(xb[:, at0:at0 + w], keys[:, c * CHUNK:(c + 1) * CHUNK],
                                          hqp[l % 2][:, c * w:(c + 1) * w], start=True, stop=True)
                mm.then_inc(lv_done, 1)

            def keys_turn(h):
                pe.wait_ge(kr_ready, h)
                pe.wait_ge(vtok_done, h)
                per_chunk(NCH - 1, lambda c, ch: nc.tensor.transpose(xa[:, ch], hg["kr"][:, ch], ident[:])).then_inc(ktr_done, 1)

            def chunk_states(h):
                pe.wait_ge(krt_done, h)
                per_chunk(NCH - 1, lambda c, ch: nc.tensor.matmul(
                    xa[:, ch], hg["krt"][:, ch], hg["vtok"][:, ch], start=True, stop=True)).then_inc(ds_done, 1)

            def head_output(h):
                pe.wait_ge(lv_free, (LEVELS + 1) * h)
                pe.wait_ge(state_ready, h)

                def product(c, ch):
                    mm = nc.tensor.matmul(xb[:, ch], hg["vtok"][:, ch], hg["attn"][:, ch], start=True, stop=c == 0)
                    if c:
                        before = slice((c - 1) * CHUNK, c * CHUNK)
                        mm = nc.tensor.matmul(xb[:, ch], hg["state"][:, before], hg["qpf"][:, ch], start=False, stop=True)
                    return mm

                per_chunk(NCH, product).then_inc(out_done, 1)

            def head_stat(h):
                pe.wait_ge(osq_done, h)
                for n in range(2):
                    cols = slice(n * HALF, (n + 1) * HALF)
                    mm = nc.tensor.matmul(xa[:, cols], ones[:], hg["osq"][:, cols], start=True, stop=True)
                mm.then_inc(hstat_done, 1)

            def tiles_beside_tail(m, h):
                take(m, 0)
                half_of(0, 0)
                level(h - 1, LEVELS)
                keys_turn(h)
                half_of(0, 1).then_inc(mm_done, 1)
                chunk_states(h)
                take(m, 1)
                half_of(1, 0)
                head_output(h)
                half_of(1, 1).then_inc(mm_done, 1)
                head_stat(h)

            for h in runs(pe, KB):
                m = N_HG // 2 + 2 * h
                if first(h):
                    full_tile(m, 0)
                    full_tile(m, 1)
                else:
                    tiles_beside_tail(m, h)
                take(m + 1, 0)
                half_of(0, 0)
                pe.wait_ge(evac[1], m + 1)
                if not first(h):
                    pe.wait_ge(oc_done, h)
                per_chunk(NCH, lambda c, ch: nc.tensor.matmul(
                    xb[:, ch], hg["k"][:, ch], hg["q"][:, ch], start=True, stop=True)).then_inc(diag_done, 1)
                level(h, 1)
                half_of(0, 1).then_inc(mm_done, 1)
                level(h, 2)
                level(h, 3)
                take(m + 1, 1)
                half_of(1, 0)
                level(h, 4)
                half_of(1, 1).then_inc(mm_done, 1)
                level(h, 5)
                level(h, 6)
                pe.wait_ge(evac[0], m + 2)
                if not first(h):
                    pe.wait_ge(hy_ready, h)
                per_chunk(NCH, lambda c, ch: nc.tensor.transpose(xa[:, ch], hg["vt"][:, ch], ident[:])).then_inc(vtr_done, 1)

            tiles_beside_tail(N_GATE // 2, KB)
            with pe.Fori(N_GATE // 2 + 1, N_BR // 2) as m:
                full_tile(m, 0)
                full_tile(m, 1)

            def all_tokens_sum(acc, ready, count, done):
                pe.wait_ge(ready, count)
                for n in range(2):
                    cols = slice(n * HALF, (n + 1) * HALF)
                    mm = nc.tensor.matmul(xa[:, cols], ones[:], acc[:, cols], start=True, stop=True)
                mm.then_inc(done, 1)

            all_tokens_sum(cmu, csum_ready, KB, cmean_mm)
            for i in range(6):
                pe.wait_ge(y_split, 4 * (i + 1))
                half_tiles((N_BR + KB * i) // 2, (N_BR + KB * (i + 1)) // 2, yb_hi[i % 2], yb_lo[i % 2])
                if i == 0:
                    all_tokens_sum(crs, cvar_ready, KB, cvar_mm)

            def norm_stat(h, q):
                pe.wait_ge(nacc_ready[h], q)
                nc.tensor.matmul(spare[h], ones[:], nacc[h][:], start=True, stop=True).then_inc(nstat_done[h], 1)

            def with_norm(n0, hi, lo, h=None, q=None):
                m = n0 // 2
                if h is None:
                    half_tiles(m, m + 4, hi, lo)
                    return
                half_tiles(m, m + 1, hi, lo)
                norm_stat(h, q)
                half_tiles(m + 1, m + 3, hi, lo)
                norm_stat(h, q + 1)
                half_tiles(m + 3, m + 4, hi, lo)

            pe.wait_ge(mg_split, 8)
            with_norm(N_MIX, hx_hi[0], hx_lo[0])
            pe.wait_ge(mg_split, 16)
            with_norm(N_MIX + KB, hx_hi[1], hx_lo[1], 0, 1)
            pe.wait_ge(hx_split, 4)
            with_norm(N_Q, hx_hi[0], hx_lo[0], 1, 1)
            pe.wait_ge(hx_split, 8)
            with_norm(N_Q + KB, hx_hi[1], hx_lo[1])

            def scores(h, hd):
                for st in range(ST):
                    c = (h * XA_HEADS + hd) * ST + st
                    if c >= 2:
                        pe.wait_ge(exp_done, c - 1)
                    bank = xb[:, (c % 2) * HALF:(c % 2) * HALF + M]
                    rows = slice(st * P, (st + 1) * P)
                    for k in range(2):
                        t = 2 * hd + k
                        mm = mm3(bank, yb_hi[h][:, t, rows], yb_lo[h][:, t, rows], kh[:, t], kl[:, t], k == 0, k == 1)
                    mm.then_inc(sc_done, 1)

            def probs_turn(h, hd):
                i = h * XA_HEADS + hd
                pe.wait_ge(p_ready, ST * (i + 1))
                for mt in range(MT):
                    for st in range(ST):
                        at0 = mt * HALF + st * P
                        mm = nc.tensor.transpose(xa[:, at0:at0 + P], prob[i % 2][:, st, mt * P:(mt + 1) * P], ident[:])
                mm.then_inc(tr_done, 1)

            def values(h, hd):
                i = h * XA_HEADS + hd
                pe.wait_ge(pt_split, i + 1)
                if i:
                    pe.wait_ge(o_split, 2 * i)
                for dt in range(2):
                    t = 2 * hd + dt
                    for mt in range(MT):
                        w = slice(t * P, (t + 1) * P)
                        mm = mm3(spare[dt], vh[:, mt, w], vl[:, mt, w], pt_hi[:, mt], pt_lo[:, mt], mt == 0, mt == MT - 1)
                    mm.then_inc(pv_done, 1)

            pe.wait_ge(kv_loaded, 64)
            for h in range(2):
                for u in range(2):
                    pe.wait_ge(evac[u], (N_Q + KB * (h + 1)) // 2)
                scores(h, 0)
                for hd in range(XA_HEADS):
                    if hd + 1 < XA_HEADS:
                        scores(h, hd + 1)
                    probs_turn(h, hd)
                    values(h, hd)
            pe.wait_ge(o_split, 8)
            with_norm(N_WO, yb_hi[0], yb_lo[0])
            pe.wait_ge(o_split, 16)
            with_norm(N_WO + KB, yb_hi[1], yb_lo[1], 0, 3)

            for h in range(2):
                n0 = N_MLP + h * 2 * FFB * KB
                pe.wait_ge(hx_split, 8 + 4 * (h + 1))
                for kind, b in MLP_ORDER:
                    if kind == "up":
                        if b == 0 and h == 0:
                            with_norm(n0, yb_hi[h], yb_lo[h], 1, 3)
                        elif b == 0:
                            half_tiles(n0 // 2, n0 // 2 + 1, yb_hi[h], yb_lo[h])
                            norm_stat(0, 5)
                            half_tiles(n0 // 2 + 1, n0 // 2 + 4, yb_hi[h], yb_lo[h])
                        else:
                            with_norm(n0, yb_hi[h], yb_lo[h])
                    else:
                        pe.wait_ge(ff_split, KB * (FFB * h + b + 1))
                        with_norm(n0, hx_hi[b % 2], hx_lo[b % 2])
                    n0 += KB
            norm_stat(1, 5)

        @block.vector
        def _(dve):
            v = nc.vector
            s = Steps(dve, dve_step)

            def done(ins):
                s.wait(s.at(ins))

            def low(out, full, hi):
                return v.tensor_tensor(out, full, hi.bitcast(F32), ALU.subtract)

            def scaled(out, x, gain, r):
                return v.scalar_tensor_tensor(out, x, gain, r, ALU.mult, ALU.mult)

            def newton(y, t, total, scale):
                done(v.scalar_tensor_tensor(t, total, EPS / scale, t, ALU.add, ALU.mult))
                return v.scalar_tensor_tensor(y, t, 1.5, y, ALU.subtract, ALU.mult)

            def add(out, a, b):
                return v.tensor_tensor(out, a, b, ALU.add)

            def mul(out, a, b):
                return v.tensor_tensor(out, a, b, ALU.mult)

            def sub(out, a, b):
                return v.tensor_tensor(out, a, b, ALU.subtract)

            def affine(out, x, a, b):
                return v.tensor_scalar(out, x, a, b, ALU.mult, ALU.add)

            def neg_gain(gain, c):
                return der[:, NEG + NEG_GAINS.index(gain), bass.ds(c, 1)]

            v.memset(ones[:], 1.0)
            v.memset(eps, EPS)
            dve.wait_ge(consts_in, 48)
            LB, LB1, CA, TE, TW, TZ, TZ2, TP, TM, TR = (der[:, i] for i in range(10))
            v.tensor_copy(lvmask[:], mask_f[:])
            sub(TM, par[:, :, HLB], par[:, :, HLB]).then_inc(consts_ready, 1)
            dve.wait_ge(exps_ready, 1)
            done(v.reciprocal(TR, TE))
            done(mul(TM, TE, TR))
            done(sub(LB, TM, TM))
            affine(LB1, LB, -1.0, 1.0)
            for i, gain in enumerate(NEG_GAINS):
                v.tensor_scalar(der[:, NEG + i], par[:, :, gain], -1.0, None, ALU.mult)
            done(v.tensor_scalar(TZ, TW, 2.0, None, ALU.add))
            done(v.reciprocal(TZ, TZ))
            done(mul(TZ, TW, TZ))
            done(mul(TZ2, TZ, TZ))
            done(v.tensor_scalar(TP, TZ2, 1.0 / 15.0, None, ALU.mult))
            for c in (13, 11, 9, 7, 5, 3):
                done(v.scalar_tensor_tensor(TP, TP, 1.0 / c, TZ2, ALU.add, ALU.mult))
            done(v.scalar_tensor_tensor(TP, TP, 1.0, TZ, ALU.add, ALU.mult))
            done(v.tensor_scalar(TM, par[:, :, LRU_LAM], -1.0, 0.0, ALU.mult, ALU.max))
            done(v.scalar_tensor_tensor(TM, TP, 2.0, TM, ALU.mult, ALU.add))
            done(v.tensor_scalar(CA, TM, -LRU_C, None, ALU.mult))

            dve.wait_ge(mem_sq_done, 1)
            v.tensor_reduce(m_acc[:], mem_sq[:].rearrange("p k m -> p m k"), AX_X, ALU.add).then_inc(mem_acc_done, 1)
            dve.wait_ge(mem_rt, 1)
            done(newton(m_r[:], m_acc[:], xa[:, 0:M], 1.0 / D))
            for k in range(KB):
                scaled(mem[:, k], mem[:, k], neg_gain(G_MEM, k), m_r[:]).then_inc(mem_normed, 1)
            dve.wait_ge(mem_hi_done, 1)
            low(mem_lo[:], mem[:], mem_hi[:]).then_inc(mem_split, 1)
            for k in range(KB):
                dve.wait_ge(xsq_done, k + 1)
                if k == 0:
                    ins = v.tensor_copy(x_acc[:], xsq[:, 0])
                else:
                    dve.wait_ge(xacc_done, k)
                    ins = add(x_acc[:], x_acc[:], xsq[:, k % 2])
                ins.then_inc(xacc_done, 1)
            with dve.Fori(0, KB // 2) as m:
                for u in range(2):
                    dve.wait_ge(kv_hi_done, 2 * m + u + 1)
                    t = bass.ds(2 * m + u, 1)
                    low(kv_sb[1][:, t], ps[u][:, 0:M], kv_sb[0][:, t]).then_inc(evac[u], 1)
            dve.wait_ge(x_rt, 1)
            done(newton(x_r[:], x_acc[:], xb[:], 1.0 / D))
            with dve.Fori(0, KB // 2) as j:
                for u in range(2):
                    t = bass.ds(2 * j + u, 1)
                    scaled(ht[:, u], x_sb[:, t], neg_gain(G_PRE_MIX, 2 * j + u), x_r[:]).then_inc(h_normed, 1)
                for u in range(2):
                    n = KB + 2 * j + u
                    dve.wait_ge(kv_hi_done, n + 1)
                    cols = bass.ds((2 * j + u) * P, P)
                    low(kv_sb[3][:, :, cols], ps[u][:, 0:M].rearrange("p (m n) -> p m n", n=P),
                        kv_sb[2][:, :, cols]).then_inc(evac[u], 1)
                for u in range(2):
                    t = bass.ds(2 * j + u, 1)
                    dve.wait_ge(h_hi_done, 2 * j + u + 1)
                    low(h_lo[:, t], ht[:, u], h_hi[:, t]).then_inc(h_split, 1)
                dve.wait_ge(h_split, 2 * j + 2)

            def conv_taps(src, c, taps, base):
                for j in taps:
                    w = pc(c, CONF_W + j)
                    acc = cacc[j % 2][:]
                    if j >= 2:
                        s.wait(base + j - 1)
                        ins = v.scalar_tensor_tensor(acc, src[:, j:j + T], w, acc, ALU.mult, ALU.add)
                    elif j == 0:
                        ins = affine(acc, src[:, 0:T], w, pc(c, CONF_B))
                    else:
                        ins = v.tensor_scalar(acc, src[:, j:j + T], w, None, ALU.mult)
                    s.at(ins)
                return base + CW

            def conv_end(q, stored, last):
                if stored:
                    dve.wait_ge(conv_stored, 16 * q)
                s.wait(last)
                add(cout[:], cacc[0][:], cacc[1][:]).then_inc(conv_done, 1)
                dve.wait_ge(conv_done, q + 1)
                if stored:
                    dve.wait_ge(csum_ready, q)
                add(cmu[:], cmu[:], cout[:]).then_inc(csum_ready, 1)

            dve.wait_ge(kv_stored, 64)
            for p in range(2):
                v.memset(ub[p][:, 0:PAD], 0.0)
            done(v.memset(cmu[:], 0.0))
            s.loop(CW)
            for i in runs(dve, KB // 2):
                s.body(i)
                m = N_CONF // 2 + 2 * i
                dve.wait_ge(evac[1], m + 1)
                mul(ub[0][:, PAD:], ps[0][:], sigb[:]).then_inc(evac[0], 1)
                dve.wait_ge(evac[0], m + 1)
                base = s.base
                conv_taps(ub[0], 2 * i, range(16), base)
                dve.wait_ge(evac[1], m + 2)
                if not first(i):
                    dve.wait_ge(glu_stored, 16 * i)
                mul(ub[1][:, PAD:], ps[0][:], sigb[:]).then_inc(evac[0], 1)
                last = conv_taps(ub[0], 2 * i, range(16, CW), base)
                conv_end(i, not first(i), last)
            s.end(KB // 2)

            for p in range(2):
                done(v.memset(lxb[p][:, 0:LW - 1], 0.0))
            s.loop(13)
            with dve.Fori(0, KB // 2) as b:
                s.body(b)
                m = N_LRU // 2 + 2 * b
                dve.wait_ge(lg_loaded, 16 * b + 16)
                done(v.tensor_copy(lg_hi[:], lg_raw[:]))
                low(lg_lo[:], lg_raw[:], lg_hi[:]).then_inc(lg_split, 1)
                for p in range(2):
                    c = 2 * b + p
                    dve.wait_ge(evac[p], m + 1)
                    done(affine(lxc[:, p], lxb[p][:, 0:T], pc(c, LRU_W), pc(c, LRU_B)))
                    for j in range(1, LW):
                        ins = v.scalar_tensor_tensor(lxc[:, p], lxb[p][:, j:j + T], pc(c, LRU_W + j), lxc[:, p], ALU.mult, ALU.add)
                        if j < LW - 1:
                            done(ins)
                    ins.then_inc(xc_ready, 1)
                for p in range(2):
                    dve.wait_ge(xc_hi_done, 2 * b + p + 1)
                    low(lxc_lo[:, p], lxc[:, p], lxc_hi[:, p]).then_inc(lru_split, 1)
                gated = []
                for p in range(2):
                    dve.wait_ge(lgate_done, 4 * b + 2 * p + 2)
                    ca = der[:, 2, bass.ds(2 * b + p, 1)]
                    v.tensor_scalar(lga[:, p], lga[:, p], ca, -1e-6, ALU.mult, ALU.min).then_inc(la_ready, 1)
                    gated.append(s.at(mul(lgx[:, p], lgx[:, p], lxc[:, p])))
                for p in range(2):
                    dve.wait_ge(ldec_done, 2 * b + p + 1)
                    v.scalar_tensor_tensor(ltanh[:, p], lsq[:, p], 1.0, ltanh[:, p], ALU.add, ALU.mult).then_inc(lm_ready, 1)
                for p in range(2):
                    dve.wait_ge(lmult_done, 2 * b + p + 1)
                    s.wait(gated[p])
                    done(mul(lgx[:, p], lgx[:, p], lsq[:, p]))
                    s.wait(s.at(v.tensor_tensor_scan(lga[:, p], ldec[:, p], lgx[:, p], 0.0, ALU.mult, ALU.add)))
                    dve.wait_ge(evac[p], m + 2)
                    mul(lgel[:, p], lga[:, p], lgel[:, p]).then_inc(ylru_ready, 1)
            s.end(KB // 2)

            def sides(t, c):
                both = t[:].rearrange("p (n two c) -> p n two c", two=2, c=c)
                return both[:, :, 0], both[:, :, 1]

            def all_blocks(x, c):
                return x.to_broadcast([P, HALF // c, c])

            zc, sp_, sn, f, b, k, q, gg = (hg[x] for x in ("zc", "sp", "sn", "f", "b", "k", "q", "gg"))

            def queries(h, l, last):
                c = 2 ** (l - 1)
                s.wait(last)
                if l > 1:
                    mul(sides(hg[f"kp{l % 2}"], c)[0], sides(k, c)[0], sides(b, c)[0])
                mul(hqp[l % 2][:].rearrange("p (n c) -> p n c", c=c), sides(q, c)[1], sides(f, c)[1]).then_inc(lv_ready, 1)

            def widen(h, l):
                c = 2 ** (l - 1)
                bl, _ = sides(b, c)
                fl, fr = sides(f, c)
                dve.wait_ge(lv_ready, LEVELS * h + l)
                if l == 1:
                    done(v.tensor_copy(bl, fr))
                else:
                    done(mul(bl, bl, all_blocks(fr[:, :, c - 1:c], c)))
                return s.at(mul(fr, fr, all_blocks(fl[:, :, c - 1:c], c)))

            def scores_out(h, l):
                c = 2 ** (l - 1)
                dve.wait_ge(lv_done, LEVELS * h + l)
                v.memset(small[:, 14:15], 0.0)
                chunks = hg["attn"][:].rearrange("p (ch n two c) -> p ch n two c", ch=NCH, two=2, c=c)
                mask = lvmask[:, l - 1].rearrange("p (o n c) -> p o n c", o=1, c=c).to_broadcast([P, NCH, CHUNK // 2 // c, c])
                bank = xb[:, (l % 2) * HALF:(l % 2 + 1) * HALF].rearrange("p (ch n c) -> p ch n c", ch=NCH, c=c)
                v.copy_predicated(chunks[:, :, :, 1], mask, bank).then_inc(lv_free, 1)

            def states(h):
                dve.wait_ge(ds_done, h)
                done(v.tensor_copy(hg["state"][:, 0:CHUNK], xa[:, 0:CHUNK]))
                for c in range(1, NCH - 1):
                    ch = slice(c * CHUNK, (c + 1) * CHUNK)
                    ins = v.scalar_tensor_tensor(hg["state"][:, ch], hg["state"][:, (c - 1) * CHUNK:c * CHUNK],
                                                 f[:, (c + 1) * CHUNK - 1:(c + 1) * CHUNK], xa[:, ch], ALU.mult, ALU.add)
                    if c < NCH - 2:
                        done(ins)
                ins.then_inc(state_ready, 1)

            def gated_output(h, m):
                dve.wait_ge(evac[1], m)
                dve.wait_ge(oc_done, h)
                return s.at(v.scalar_tensor_tensor(gg[:], gg[:], -1.0, hg["oc"][:], ALU.mult, ALU.mult))

            def normed_output(h, gated):
                dve.wait_ge(hrt_done, h)
                done(newton(hg["rt"][:], hg["nw"][:], xa[:], 1.0 / P))
                s.wait(gated)
                mul(gg[:], gg[:], hg["rt"][:]).then_inc(hy_ready, 1)

            def head(h):
                m = N_HG // 2 + 2 * h
                if not first(h):
                    scores_out(h - 1, LEVELS)
                dve.wait_ge(mm_done, 2 * m + 1)
                v.tensor_scalar(zc[:], ps[0][:], CLIP, -CLIP, ALU.min, ALU.max).then_inc(evac[0], 1)
                if not first(h):
                    states(h)
                    dve.wait_ge(state_ready, h)
                lb, lb1 = (der[:, i, bass.ds(h, 1)] for i in (0, 1))
                dve.wait_ge(hsig, 2 * h + 2)
                done(v.scalar_tensor_tensor(f[:], sn[:], lb, sp_[:], ALU.mult, ALU.add))
                s.at(v.tensor_scalar(f[:], f[:], 1.0, None, ALU.min))
                s.at(v.tensor_scalar(k[:], sn[:], lb1, 0.0, ALU.mult, ALU.max))
                last = s.at(v.memset(sides(b, 1)[1], 1.0))
                if not first(h):
                    gated = gated_output(h, m)
                dve.wait_ge(hsigq, h + 1)
                v.scalar_tensor_tensor(q[:], ps[1][:], DK_SCALE, hg["qs"][:], ALU.mult, ALU.mult).then_inc(evac[1], 1)
                dve.wait_ge(evac[1], m + 1)
                queries(h, 1, last)
                last = widen(h, 1)
                queries(h, 2, last)
                if not first(h):
                    normed_output(h, gated)
                dve.wait_ge(diag_done, h + 1)
                v.tensor_tensor(hg["attn"][:].rearrange("p (n c) -> p n c", c=CHUNK), xb[:].rearrange("p (n c) -> p n c", c=CHUNK),
                                ident[:].rearrange("p (o c) -> p o c", o=1).to_broadcast([P, NCH, CHUNK]), ALU.mult).then_inc(lv_free, 1)
                dve.wait_ge(lv_free, (LEVELS + 1) * h + 1)
                scores_out(h, 1)
                for l in range(2, LEVELS):
                    last = widen(h, l)
                    queries(h, l + 1, last)
                    if l == 5:
                        dve.wait_ge(hsigg, h + 1)
                        dve.wait_ge(hy_free, h + 1)
                        v.scalar_tensor_tensor(gg[:], ps[1][:], pc(h, HG_G), sp_[:], ALU.mult, ALU.mult).then_inc(evac[1], 1)
                    scores_out(h, l)
                s.wait(widen(h, LEVELS))
                mul(hg["kr"][:], k[:], b[:]).then_inc(kr_ready, 1)
                s.at(mul(hg["qpf"][:], q[:], f[:]))

            dve.wait_ge(ylru_ready, KB)
            dve.wait_ge(ylru_stored, 16 * KB // 2)
            for t in ("b", "kp0", "kp1"):
                done(v.memset(hg[t][:], 1.0))
            head(0)
            s.loop(28, start=1)
            with dve.Fori(1, KB) as h:
                s.body(h)
                head(h)
            s.end(KB)
            scores_out(KB - 1, LEVELS)
            states(KB)
            normed_output(KB, gated_output(KB, N_GATE // 2))

            def split_branch(idx, j):
                q = 4 * idx + j
                dve.wait_ge(y_loaded, 16 * q + 16)
                t = bass.ds(2 * j, 2)
                if idx % 3 == 2:
                    cols = slice((idx // 3) * HALF, (idx // 3 + 1) * HALF)
                    for u in range(2):
                        done(sub(yst[:, u], cmu[:, cols], yst[:, u]))
                        mul(yst[:, u], yst[:, u], crs[:, cols]).then_inc(y_pre, 1)
                dve.wait_ge(y_hi_done, q + 1)
                low(yb_lo[idx % 2][:, t], yst[:], yb_hi[idx % 2][:, t]).then_inc(y_split, 1)

            v.memset(ub[0][:, 0:PAD], 0.0)
            done(v.memset(crs[:], 0.0))
            s.loop(CW)
            with dve.Fori(0, KB // 2) as i:
                s.body(i)
                dve.wait_ge(glu_loaded, 16 * i + 16)
                last = conv_taps(ub[0], 2 * i + 1, range(CW), s.base)
                conv_end(i + KB // 2, True, last)
                split_branch(0, i)
            s.end(KB // 2)

            dve.wait_ge(cmean_ready, 1)
            for idx in range(6):
                h, br = idx // 3, idx % 3
                s.loop(2 if idx in (1, 4) else 0)
                with dve.Fori(0, KB // 2) as j:
                    s.body(j)
                    if idx < 5:
                        split_branch(idx + 1, j)
                    if idx == 0:
                        for u, buf in enumerate((cout, gbuf)):
                            dve.wait_ge(cdev_loaded, 32 * j + 32)
                            sub(buf[:], buf[:], cmu[:]).then_inc(cdev_ready, 1)
                        for u, buf in enumerate((cout, gbuf)):
                            dve.wait_ge(cdev_sq, 2 * j + u + 1)
                            if u:
                                dve.wait_ge(cvar_ready, 2 * j + 1)
                            add(crs[:], crs[:], buf[:]).then_inc(cvar_ready, 1)
                        dve.wait_ge(cvar_ready, 2 * j + 2)
                    m = N_BR // 2 + 4 * idx + j
                    q = 4 * idx + j
                    dve.wait_ge(g_loaded, 16 * q + 16)
                    for u in range(2):
                        dve.wait_ge(mm_done, 2 * m + u + 1)
                        mul(gst[:, u], ps[u][:, 0:HALF], gst[:, u]).then_inc(evac[u], 1)
                    if idx:
                        dve.wait_ge(g_used, 8 * idx)
                    for u in range(2):
                        dve.wait_ge(evac[u], m + 1)
                        t = bass.ds(2 * j + u, 1)
                        if br == 0:
                            ins = v.tensor_copy(macc[:, t], gst[:, u])
                        else:
                            ins = add(macc[:, t], macc[:, t], gst[:, u])
                        ins.then_inc(g_used, 1)
                    if br == 2:
                        for u in range(2):
                            t = bass.ds(2 * j + u, 1)
                            dve.wait_ge(mg_hi_done, KB * h + 2 * j + u + 1)
                            low(hx_lo[h][:, t], macc[:, t], hx_hi[h][:, t]).then_inc(mg_split, 1)
                s.end(KB // 2)
                if idx == 0:
                    dve.wait_ge(cstd_ready, 1)
                    done(newton(crs[:], cout[:], xa[:], 1.0 / D))

            def sum_out(turn, h, j):
                n = KB * turn + 2 * j
                for u in range(2):
                    t = 2 * j + u
                    dve.wait_ge(sq_done, n + u + 1)
                    if t == KB - 1:
                        v.tensor_copy(xx[h][:, t], ps[u][:, 0:HALF]).then_inc(evac[u], 1)
                    if t == 0:
                        ins = v.tensor_copy(nacc[h][:], sqm[:, u])
                    else:
                        ins = add(nacc[h][:], nacc[h][:], sqm[:, u])
                    if t < KB - 1:
                        done(ins)
                        v.tensor_copy(xx[h][:, t], ps[u][:, 0:HALF]).then_inc(evac[u], 1)
                    else:
                        ins.then_inc(nacc_ready[h], 1)

            def recip(h, q):
                dve.wait_ge(nrt_done[h], q)
                done(newton(rn[h][:], nacc[h][:], spare[h], 1.0 / D))

            def new_squares(c, j):
                h = c % 2
                dve.wait_ge(xnsq_done, 4 * c + j + 1)
                if j == 0:
                    ins = add(nacc[h][:], nt[:, 0], nt[:, 1])
                else:
                    done(add(nacc[h][:], nacc[h][:], nt[:, 0]))
                    ins = add(nacc[h][:], nacc[h][:], nt[:, 1])
                if j < 3:
                    ins.then_inc(xn_used, 1)
                    dve.wait_ge(xn_used, 3 * c + j + 1)
                else:
                    ins.then_inc(nacc_ready[h], 1)

            def residual(c, pairs):
                h, gain = c % 2, (G_POST_MIX, G_POST_XA, G_POST_MLP)[c // 2]
                for j in pairs:
                    for u in range(2):
                        t = 2 * j + u
                        last = s.at(scaled(xx[h][:, t], xx[h][:, t], par[:, t, gain:gain + 1], rn[h][:]))
                    s.wait(last)
                    dve.wait_ge(xs_loaded, 16 * (4 * c + j + 1))
                    sub(xx[h][:, 2 * j:2 * j + 2], xs[:], xx[h][:, 2 * j:2 * j + 2]).then_inc(x_new, 1)
                    if c < 4 and j:
                        new_squares(c, j - 1)
                if c < 4 and 3 in pairs:
                    new_squares(c, 3)

            def renorm(c, pairs):
                h, gain = c % 2, (G_PRE_XA, G_PRE_MLP)[c // 2]
                hi, lo = ((hx_hi, hx_lo), (yb_hi, yb_lo))[c // 2]
                dve.wait_ge(x_new, 4 * c + 4)
                if pairs[0]:
                    dve.wait_ge(hx_split, 4 * c + pairs[0])
                for j in pairs:
                    tmp = (nt, xs)[j % 2]
                    for u in range(2):
                        t = 2 * j + u
                        ins = scaled(tmp[:, u], xx[h][:, t], neg_gain(gain, t), rn[h][:])
                    ins.then_inc(hn_ready, 1)
                for j in pairs:
                    tmp = (nt, xs)[j % 2]
                    dve.wait_ge(hn_hi_done, 4 * c + j + 1)
                    low(lo[h][:, 2 * j:2 * j + 2], tmp[:], hi[h][:, 2 * j:2 * j + 2]).then_inc(hx_split, 1)

            def beside(c, q, pair):
                h = c % 2
                pair(0)
                recip(h, q)
                residual(c, (0, 1))
                pair(1)
                residual(c, (2, 3))
                pair(2)
                if c < 4:
                    recip(h, q + 1)
                    renorm(c, (0, 1))
                pair(3)
                if c < 4:
                    renorm(c, (2, 3))

            def queries_out(h, j):
                for u in range(2):
                    t = 2 * j + u
                    dve.wait_ge(q_hi_done, KB * h + t + 1)
                    low(yb_lo[h][:, t], ps[u][:, 0:HALF], yb_hi[h][:, t]).then_inc(evac[u], 1)

            for j in range(4):
                sum_out(0, 0, j)
            beside(0, 1, lambda j: sum_out(1, 1, j))
            beside(1, 1, lambda j: queries_out(0, j))
            for j in range(4):
                queries_out(1, j)

            def softmax_stat(i, st):
                c = ST * i + st
                bank = xb[:, (c % 2) * HALF:(c % 2) * HALF + M]
                dve.wait_ge(sc_done, c + 1)
                done(v.tensor_reduce(small[:, c % 4:c % 4 + 1], bank, AX_X, ALU.max))
                v.tensor_scalar(small[:, 4 + c % 4:5 + c % 4], small[:, c % 4:c % 4 + 1], -XA_SCALE, None, ALU.mult).then_inc(nmax_ready, 1)

            def softmax_div(i, st):
                c = ST * i + st
                total = small[:, 8 + c % 4:9 + c % 4]
                dve.wait_ge(exp_done, c + 1)
                done(v.reciprocal(total, total))
                v.tensor_scalar(prob[i % 2][:, st], prob[i % 2][:, st], total, None, ALU.mult).then_inc(p_ready, 1)

            def softmax(i):
                softmax_stat(i, 0)
                for st in range(1, ST):
                    softmax_stat(i, st)
                    softmax_div(i, st - 1)
                softmax_div(i, ST - 1)

            for h in range(2):
                softmax(h * XA_HEADS)
                for hd in range(XA_HEADS):
                    i = h * XA_HEADS + hd
                    if hd + 1 < XA_HEADS:
                        softmax(i + 1)
                    dve.wait_ge(pt_hi_done, i + 1)
                    low(pt_lo[:], xa[:].rearrange("p (m n) -> p m n", m=MT), pt_hi[:]).then_inc(pt_split, 1)
                    for dt in range(2):
                        t = 2 * hd + dt
                        dve.wait_ge(o_hi_done, 2 * i + dt + 1)
                        low(yb_lo[h][:, t], spare[dt], yb_hi[h][:, t]).then_inc(o_split, 1)

            dve.wait_ge(x_stored, 16 * 8)
            for j in range(4):
                sum_out(2, 0, j)
            beside(2, 3, lambda j: sum_out(3, 1, j))

            def up_out(m, h, b, j):
                for u in range(2):
                    n = KB * (FFB * h + b) + 2 * j + u
                    dve.wait_ge(relu_done, n + 1)
                    mul(sqm[:, u], sqm[:, u], ps[u][:, 0:HALF]).then_inc(evac[u], 1)
                for u in range(2):
                    n = KB * (FFB * h + b) + 2 * j + u
                    t = bass.ds(2 * j + u, 1)
                    dve.wait_ge(ff_hi_done, n + 1)
                    low(hx_lo[b % 2][:, t], sqm[:, u], hx_hi[b % 2][:, t]).then_inc(ff_split, 1)

            def wait_sum(m):
                for u in range(2):
                    dve.wait_ge(evac[u], m)

            def down_out(m, h, j):
                for u in range(2):
                    t = bass.ds(2 * j + u, 1)
                    dve.wait_ge(mm_done, 2 * m + u + 1)
                    add(xx[h][:, t], xx[h][:, t], ps[u][:, 0:HALF]).then_inc(evac[u], 1)

            for h in range(2):
                m0 = (N_MLP + h * 2 * FFB * KB) // 2
                for kind, b in MLP_ORDER:
                    if kind == "up" and b == 0:
                        c = 3 + h
                        beside(c, (3, 5)[h], lambda j: up_out(m0 + j, h, b, j))
                    elif kind == "up":
                        with dve.Fori(0, KB // 2) as j:
                            up_out(m0 + j, h, b, j)
                    elif 0 < b < FFB - 1:
                        wait_sum(m0)
                        with dve.Fori(0, KB // 2) as j:
                            down_out(m0 + j, h, j)
                    elif b:
                        wait_sum(m0)
                        for j in range(KB // 2):
                            down_out(m0 + j, h, j)
                            dve.wait_ge(ysq_done, 4 * h + j + 1)
                            if j == 0:
                                done(add(nacc[h][:], sqm[:, 0], sqm[:, 1]))
                            else:
                                done(add(nacc[h][:], nacc[h][:], sqm[:, 0]))
                                ins = add(nacc[h][:], nacc[h][:], sqm[:, 1])
                                if j < 3:
                                    done(ins)
                                else:
                                    ins.then_inc(nacc_ready[h], 1)
                    m0 += KB // 2
            beside(5, 5, lambda j: None)

        @block.scalar
        def _(act):
            a = nc.scalar
            s = Steps(act, act_step)

            def done(ins):
                s.wait(s.at(ins))

            def copy(out, x, scale=1.0):
                return a.activation(out, x, ACT.Copy, scale=scale)

            def rsqrt(y, t, x, scale):
                done(a.activation(y, x, ACT.Abs_reciprocal_sqrt, bias=eps, scale=scale))
                return a.activation(t, y, ACT.Square, scale=(scale / 2) ** 0.5)

            act.wait_ge(mem_in, 16)
            a.activation(mem_sq[:], mem[:], ACT.Square).then_inc(mem_sq_done, 1)
            act.wait_ge(consts_ready, 1)
            done(a.activation(der[:, 4], par[:, :, LRU_LAM], ACT.Abs))
            a.activation(der[:, 3], der[:, 8], ACT.Exp)
            a.activation(der[:, 4], der[:, 4], ACT.Exp, scale=-1.0).then_inc(exps_ready, 1)
            act.wait_ge(mem_stat, 1)
            rsqrt(m_r[:], m_acc[:], xa[:, 0:M], 1.0 / D).then_inc(mem_rt, 1)
            act.wait_ge(mem_normed, KB)
            copy(mem_hi[:], mem[:]).then_inc(mem_hi_done, 1)
            for k in range(KB):
                if k % 4 == 0:
                    act.wait_ge(x_in[k // 4], 16)
                if k >= 2:
                    act.wait_ge(xacc_done, k - 1)
                a.activation(xsq[:, k % 2], x_sb[:, k], ACT.Square).then_inc(xsq_done, 1)
            with act.Fori(0, KB // 2) as m:
                for u in range(2):
                    act.wait_ge(mm_done, 2 * m + u + 1)
                    copy(kv_sb[0][:, bass.ds(2 * m + u, 1)], ps[u][:, 0:M]).then_inc(kv_hi_done, 1)
            act.wait_ge(x_stat, 1)
            rsqrt(x_r[:], x_acc[:], xb[:], 1.0 / D).then_inc(x_rt, 1)
            with act.Fori(0, KB // 2) as j:
                for u in range(2):
                    act.wait_ge(h_normed, 2 * j + u + 1)
                    copy(h_hi[:, bass.ds(2 * j + u, 1)], ht[:, u]).then_inc(h_hi_done, 1)
                for u in range(2):
                    act.wait_ge(mm_done, KB + 2 * j + u + 1)
                    copy(kv_sb[2][:, :, bass.ds((2 * j + u) * P, P)],
                         ps[u][:, 0:M].rearrange("p (m n) -> p m n", n=P)).then_inc(kv_hi_done, 1)

            act.wait_ge(kv_stored, 64)
            with act.Fori(0, KB) as c:
                m = N_CONF // 2 + c
                act.wait_ge(evac[0], m)
                act.wait_ge(mm_done, 2 * m + 2)
                a.activation(sigb[:], ps[1][:], ACT.Sigmoid).then_inc(evac[1], 1)

            s.loop(2)
            for b in runs(act, KB // 2):
                s.body(b)
                m = N_LRU // 2 + 2 * b
                for p in range(2):
                    act.wait_ge(mm_done, 2 * m + p + 1)
                    copy(lxb[p][:, LW - 1:], ps[p][:]).then_inc(evac[p], 1)
                if not first(b):
                    act.wait_ge(ylru_ready, 2 * b)
                for p in range(2):
                    act.wait_ge(xc_ready, 2 * b + p + 1)
                    copy(lxc_hi[:, p], lxc[:, p]).then_inc(xc_hi_done, 1)
                if not first(b):
                    act.wait_ge(ylru_stored, 16 * b)
                for p in range(2):
                    act.wait_ge(mm_done, 2 * m + p + 3)
                    a.activation(lgel[:, p], ps[p][:], ACT.Gelu_apprx_tanh).then_inc(evac[p], 1)
                for p in range(2):
                    for g, (out_, acc, bias) in enumerate(((lgx, xa, LRU_BX), (lga, xb, LRU_BA))):
                        act.wait_ge(lmm_done, 4 * b + 2 * p + g + 1)
                        a.activation(out_[:, p], acc[:], ACT.Sigmoid, bias=pc(2 * b + p, bias)).then_inc(lgate_done, 1)
                for p in range(2):
                    act.wait_ge(la_ready, 2 * b + p + 1)
                    a.activation(ltanh[:, p], lga[:, p], ACT.Tanh, scale=-1.0)
                    done(a.activation(ldec[:, p], lga[:, p], ACT.Exp))
                    a.activation(lsq[:, p], ldec[:, p], ACT.Square).then_inc(ldec_done, 1)
                for p in range(2):
                    act.wait_ge(lm_ready, 2 * b + p + 1)
                    a.activation(lsq[:, p], ltanh[:, p], ACT.Sqrt).then_inc(lmult_done, 1)
            s.end(KB // 2)

            def state_keys(h):
                act.wait_ge(ktr_done, h)
                last = (NCH - 1) * CHUNK
                copy(hg["krt"][:, 0:last], xa[:, 0:last]).then_inc(krt_done, 1)

            def output(h):
                act.wait_ge(out_done, h)
                a.activation(hg["osq"][:], xb[:], ACT.Square).then_inc(osq_done, 1)
                copy(hg["oc"][:], xb[:]).then_inc(oc_done, 1)

            def output_norm(h):
                act.wait_ge(hstat_done, h)
                rsqrt(hg["rt"][:], hg["nw"][:], xa[:], 1.0 / P).then_inc(hrt_done, 1)

            def head(h):
                m = N_HG // 2 + 2 * h
                if not first(h):
                    state_keys(h)
                act.wait_ge(evac[0], m + 1)
                for out_, sign in ((hg["sp"], 1.0), (hg["sn"], -1.0)):
                    a.activation(out_[:], hg["zc"][:], ACT.Sigmoid, scale=sign).then_inc(hsig, 1)
                if not first(h):
                    output(h)
                act.wait_ge(mm_done, 2 * m + 2)
                a.activation(hg["qs"][:], ps[1][:], ACT.Sigmoid).then_inc(hsigq, 1)
                if not first(h):
                    output_norm(h)
                act.wait_ge(mm_done, 2 * m + 3)
                copy(hg["vt"][:], ps[0][:]).then_inc(evac[0], 1)
                act.wait_ge(lv_ready, LEVELS * h + 1)
                act.wait_ge(mm_done, 2 * m + 4)
                a.activation(hg["sp"][:], ps[1][:], ACT.Sigmoid).then_inc(hsigg, 1)
                act.wait_ge(vtr_done, h + 1)
                copy(hg["vtok"][:], xa[:]).then_inc(vtok_done, 1)

            act.wait_ge(glu_stored, 16 * KB // 2)
            act.wait_ge(conv_stored, 16 * KB // 2)
            head(0)
            s.loop(1, start=1)
            with act.Fori(1, KB) as h:
                s.body(h)
                head(h)
            s.end(KB)
            state_keys(KB)

            def branch_high(idx, j):
                q, h = 4 * idx + j, idx // 3
                if idx % 3 == 2:
                    for u in range(2):
                        act.wait_ge(y_pre, KB * h + 2 * j + u + 1)
                        c = 2 * j + u
                        ins = a.activation(yst[:, u], yst[:, u], ACT.Silu, bias=pc(c, CONF_LB), scale=pc(c, CONF_G))
                        s.at(ins)
                    s.wait(s.base + 2)
                else:
                    act.wait_ge(y_loaded, 16 * q + 16)
                copy(yb_hi[idx % 2][:, bass.ds(2 * j, 2)], yst[:]).then_inc(y_hi_done, 1)

            for i in runs(act, 4):
                for r in range(3):
                    for u, buf in enumerate((sigb, gbuf)):
                        m = N_GATE // 2 + 3 * i + r
                        if r or not first(i):
                            act.wait_ge(gate_stored[u], 48 * i + 16 * r)
                        act.wait_ge(mm_done, 2 * m + u + 1)
                        a.activation(buf[:], ps[u][:], ACT.Sigmoid).then_inc(evac[u], 1)
                        if first(i) and r == 0:
                            (output, output_norm)[u](KB)
                branch_high(0, i)
            act.wait_ge(cmean_mm, 1)
            copy(cmu[:], xa[:], 1.0 / D).then_inc(cmean_ready, 1)
            for idx in range(6):
                h = idx // 3
                act.wait_ge(mm_done, N_BR + KB * idx)
                s.loop(2 if idx in (1, 4) else 0)
                with act.Fori(0, KB // 2) as j:
                    s.body(j)
                    if idx < 5:
                        branch_high(idx + 1, j)
                    if idx == 0:
                        for u, buf in enumerate((cout, gbuf)):
                            act.wait_ge(cdev_ready, 2 * j + u + 1)
                            a.activation(buf[:], buf[:], ACT.Square).then_inc(cdev_sq, 1)
                    if idx % 3 == 2:
                        for u in range(2):
                            t = bass.ds(2 * j + u, 1)
                            act.wait_ge(g_used, KB * idx + 2 * j + u + 1)
                            copy(hx_hi[h][:, t], macc[:, t]).then_inc(mg_hi_done, 1)
                s.end(KB // 2)
                if idx == 0:
                    act.wait_ge(cvar_mm, 1)
                    rsqrt(crs[:], cout[:], xa[:], 1.0 / D).then_inc(cstd_ready, 1)

            def squares(turn, h, j):
                m = (N_MIX, N_MIX + KB, N_WO, N_WO + KB)[turn] // 2 + j
                if j == 0 and turn:
                    act.wait_ge(nacc_ready[1 - h], (0, 1, 1, 3)[turn])
                for u in range(2):
                    act.wait_ge(mm_done, 2 * m + u + 1)
                    a.activation(sqm[:, u], ps[u][:, 0:HALF], ACT.Square).then_inc(sq_done, 1)

            def norm_root(h, q):
                act.wait_ge(nstat_done[h], q)
                rsqrt(rn[h][:], nacc[h][:], spare[h], 1.0 / D).then_inc(nrt_done[h], 1)

            def load_residual(c, j):
                act.dma_start(xs[:], rows_pair(xT if c < 2 else x_d, j, c % 2)).then_inc(xs_loaded, 16)

            def new_x(c, j):
                h = c % 2
                act.wait_ge(x_new, 4 * c + j + 1)
                if j < 3:
                    load_residual(c, j + 1)
                pair = xx[h][:, 2 * j:2 * j + 2]
                if c >= 4:
                    act.dma_start(rows_pair(out, j, h), pair).then_inc(out_stored, 16)
                    return
                act.dma_start(rows_pair(x_d, j, h), pair).then_inc(x_stored, 16)
                if j:
                    act.wait_ge(xn_used, 3 * c + j)
                a.activation(nt[:], pair, ACT.Square).then_inc(xnsq_done, 1)

            def normed_high(c, j):
                hi = (hx_hi, yb_hi)[c // 2][c % 2]
                act.wait_ge(hn_ready, 4 * c + j + 1)
                copy(hi[:, 2 * j:2 * j + 2], (nt, xs)[j % 2][:]).then_inc(hn_hi_done, 1)

            def beside(c, q, pair):
                h = c % 2
                if c == 0:
                    act.wait_ge(y_split, 24)
                elif c < 5:
                    act.wait_ge(hx_split, 4 * min(c, 4))
                else:
                    act.wait_ge(x_new, 20)
                if c >= 2:
                    act.wait_ge(x_stored, 16 * 8 * (c // 2))
                load_residual(c, 0)
                pair(0)
                norm_root(h, q)
                new_x(c, 0)
                new_x(c, 1)
                pair(1)
                new_x(c, 2)
                new_x(c, 3)
                pair(2)
                if c < 4:
                    norm_root(h, q + 1)
                    normed_high(c, 0)
                    normed_high(c, 1)
                pair(3)
                if c < 4:
                    normed_high(c, 2)
                    normed_high(c, 3)

            def queries_high(h, j):
                for u in range(2):
                    t = 2 * j + u
                    act.wait_ge(mm_done, N_Q + KB * h + t + 1)
                    copy(yb_hi[h][:, t], ps[u][:, 0:HALF]).then_inc(q_hi_done, 1)

            for j in range(4):
                squares(0, 0, j)
            beside(0, 1, lambda j: squares(1, 1, j))
            beside(1, 1, lambda j: queries_high(0, j))
            for j in range(4):
                queries_high(1, j)

            def exponentials(i):
                if i >= 2:
                    act.wait_ge(tr_done, i - 1)
                for st in range(ST):
                    c = ST * i + st
                    bank = xb[:, (c % 2) * HALF:(c % 2) * HALF + M]
                    if c >= 4:
                        act.wait_ge(p_ready, c - 3)
                    act.wait_ge(nmax_ready, c + 1)
                    a.activation(prob[i % 2][:, st], bank, ACT.Exp, bias=small[:, 4 + c % 4:5 + c % 4], scale=XA_SCALE,
                                 accum_out=small[:, 8 + c % 4:9 + c % 4]).then_inc(exp_done, 1)

            for h in range(2):
                exponentials(h * XA_HEADS)
                for hd in range(XA_HEADS):
                    i = h * XA_HEADS + hd
                    if hd + 1 < XA_HEADS:
                        exponentials(i + 1)
                    act.wait_ge(tr_done, i + 1)
                    if i:
                        act.wait_ge(pv_done, 2 * i)
                    copy(pt_hi[:], xa[:].rearrange("p (m n) -> p m n", m=MT)).then_inc(pt_hi_done, 1)
                    for dt in range(2):
                        act.wait_ge(pv_done, 2 * i + dt + 1)
                        copy(yb_hi[h][:, 2 * hd + dt], spare[dt]).then_inc(o_hi_done, 1)

            for j in range(4):
                squares(2, 0, j)
            beside(2, 3, lambda j: squares(3, 1, j))

            def up_relu(m, h, b, j):
                for u in range(2):
                    n = KB * (FFB * h + b) + 2 * j + u
                    if b == 0 and h == 0 and j == 0:
                        act.wait_ge(nacc_ready[1], 3)
                    elif b == 0 and j == 0:
                        act.wait_ge(nacc_ready[0], 5)
                    else:
                        act.wait_ge(ff_split, n - 1)
                    act.wait_ge(mm_done, 2 * m + u + 1)
                    a.activation(sqm[:, u], ps[u][:, 0:HALF], ACT.Relu).then_inc(relu_done, 1)
                for u in range(2):
                    act.wait_ge(evac[u], m + 1)
                    copy(hx_hi[b % 2][:, bass.ds(2 * j + u, 1)], sqm[:, u]).then_inc(ff_hi_done, 1)

            for h in range(2):
                m0 = (N_MLP + h * 2 * FFB * KB) // 2
                for kind, b in MLP_ORDER:
                    if kind == "up" and b == 0:
                        beside(3 + h, (3, 5)[h], lambda j: up_relu(m0 + j, h, b, j))
                    elif kind == "up":
                        with act.Fori(0, KB // 2) as j:
                            up_relu(m0 + j, h, b, j)
                    elif b == 0:
                        act.wait_ge(x_stored, 16 * 16)
                        with act.Fori(0, KB // 2) as j:
                            for u in range(2):
                                act.wait_ge(mm_done, 2 * (m0 + j) + u + 1)
                                copy(xx[h][:, bass.ds(2 * j + u, 1)], ps[u][:, 0:HALF]).then_inc(evac[u], 1)
                    elif b == FFB - 1:
                        for j in range(4):
                            for u in range(2):
                                act.wait_ge(evac[u], m0 + j + 1)
                            a.activation(sqm[:], xx[h][:, 2 * j:2 * j + 2], ACT.Square).then_inc(ysq_done, 1)
                    m0 += KB // 2
            beside(5, 5, lambda j: None)

        @block.gpsimd
        def _(pool):
            nc.gpsimd.memset(small[:, 12:13], 0.0).then_inc(w_high, 1)
            pool.wait_ge(w_high, 1)
            for m in runs(pool, N_END // 2):
                for u in range(2):
                    pool.wait_ge(w_loaded[u], 16 * m + 16)
                    if not first(m):
                        pool.wait_ge(mm_done, 2 * m + u - 1)
                    nc.gpsimd.tensor_tensor(small[:, 13:14], small[:, 12:13], small[:, 12:13], ALU.add)
                    nc.gpsimd.tensor_scalar(w_hi[:, u], w_raw[:, u], 1.0, 1.0, ALU.mult, ALU.mult).then_inc(w_high, 1)
                    pool.wait_ge(w_high, 2 * m + u + 2)
                    nc.gpsimd.tensor_tensor(w_lo[:, u], w_raw[:, u], w_hi[:, u].bitcast(F32), ALU.subtract).then_inc(w_split, 1)

        @block.sync
        def _(sp):
            def weights(m, u, shift=0):
                if not first(m):
                    sp.wait_ge(w_split, 2 * m + u - 1)
                sp.dma_start(w_raw[:, u], wall[bass.ds(2 * m + u - shift, 1)].rearrange("o p n -> p (o n)")).then_inc(w_loaded[u], 16)

            def weight_tiles(n0, n1, shift=0):
                with sp.Fori(n0 // 2, n1 // 2) as m:
                    for u in range(2):
                        weights(m, u, shift)

            def weights_of(m, q):
                weights(m + q // 2, q % 2)

            sp.dma_start(mem[:], memT.rearrange("(k p) m -> p k m", p=P)).then_inc(mem_in, 16)
            sp.dma_start(par[:], params).then_inc(consts_in, 16)
            sp.dma_start(ident[:], ident_in).then_inc(consts_in, 16)
            sp.dma_start(mask_f[:], masks).then_inc(consts_in, 16)
            for m in runs(sp, KB):
                for u in range(2):
                    weights(m, u)
                if first(m):
                    for i in range(2):
                        sp.dma_start(x_sb[:, 4 * i:4 * i + 4], xT[i * HALF:(i + 1) * HALF].rearrange("(k p) n -> p k n", p=P)).then_inc(x_in[i], 16)

            def conf_store(i):
                sp.wait_ge(evac[0], N_CONF // 2 + 2 * i)
                sp.dma_start(one(glu_d, i - 1), ub[1][:, PAD:]).then_inc(glu_stored, 16)
                sp.wait_ge(conv_done, i)
                sp.dma_start(one(conv_d, 2 * i - 2), cout[:]).then_inc(conv_stored, 16)

            for i in runs(sp, KB // 2):
                m = N_CONF // 2 + 2 * i
                for q in range(4):
                    weights_of(m, q)
                if first(i):
                    for u in range(2):
                        sp.wait_ge(evac[u], KB)
                    for q in range(4):
                        sp.dma_start(kv_d[q], kv_sb[q][:].bitcast(F32).rearrange("p a b -> p (a b)")).then_inc(kv_stored, 16)
                else:
                    conf_store(i)

            def lru_store(b):
                sp.wait_ge(ylru_ready, 2 * b)
                sp.dma_start(lru_d[bass.ds(2 * b - 2, 2)].rearrange("t p n -> p t n"), lgel[:]).then_inc(ylru_stored, 16)

            for b in runs(sp, KB // 2):
                m = N_LRU // 2 + 2 * b
                for q in range(4):
                    weights_of(m, q)
                if first(b):
                    conf_store(KB // 2)
                else:
                    sp.wait_ge(lg_split, b)
                sp.dma_start(lg_raw[:].rearrange("p g k n -> p (g k n)"), one(lru_gates, b)).then_inc(lg_loaded, 16)
                if not first(b):
                    lru_store(b)

            def hgrn_store(h):
                sp.wait_ge(hy_ready, h)
                sp.dma_start(one(hgrn_d, h - 1), hg["gg"][:]).then_inc(hy_stored, 16)
                sp.wait_ge(hy_stored, 16 * h)

            sp.sem_inc(hy_free, 1)
            for h in runs(sp, KB):
                m = N_HG // 2 + 2 * h
                for q in range(4):
                    weights_of(m, q)
                if first(h):
                    lru_store(KB // 2)
                else:
                    hgrn_store(h)
                    sp.sem_inc(hy_free, 1)

            def gate_store(m):
                for u, buf in enumerate((sigb, gbuf)):
                    sp.wait_ge(evac[u], m)
                    sp.dma_start(one(gate_d, 2 * m - 2 + u - N_GATE), buf[:]).then_inc(gate_stored[u], 16)

            def load_branch(idx, j):
                sp.dma_start(yst[:], half_pair(branch_d[idx % 3], 2 * j, idx // 3)).then_inc(y_loaded, 16)

            def odd_conv_store(i):
                sp.wait_ge(conv_done, KB // 2 + i)
                sp.dma_start(one(conv_d, 2 * i - 1), cout[:]).then_inc(conv_stored, 16)

            for i in runs(sp, KB // 2):
                for r in range(3):
                    m = N_GATE // 2 + 3 * i + r
                    for u in range(2):
                        weights(m, u)
                    if r or not first(i):
                        gate_store(m)
                    if r == (2 if first(i) else 0):
                        if first(i):
                            hgrn_store(KB)
                        else:
                            odd_conv_store(i)
                            sp.wait_ge(y_split, i)
                        sp.wait_ge(csum_ready, KB // 2 + i)
                        sp.dma_start(ub[0][:, PAD:], one(glu_d, i)).then_inc(glu_loaded, 16)
                        load_branch(0, i)

            for idx in range(6):
                h, br = idx // 3, idx % 3
                for j in runs(sp, KB // 2, peel=1 if idx == 0 else 0):
                    for u in range(2):
                        weights(N_BR // 2 + 4 * idx + j, u, 24 * h)
                    if idx == 0 and first(j):
                        gate_store(N_BR // 2)
                        odd_conv_store(KB // 2)
                        sp.wait_ge(csum_ready, KB)
                        for u in range(2):
                            sp.wait_ge(gate_stored[u], 16 * 3 * KB // 2)
                        sp.wait_ge(conv_stored, 16 * KB)
                    else:
                        sp.wait_ge(g_used, 2 * (4 * idx + j))
                    sp.dma_start(gst[:], half_pair(gate_d, KB * br + 2 * j, h)).then_inc(g_loaded, 16)
                    if idx == 0:
                        if not first(j):
                            sp.wait_ge(cvar_ready, 2 * j)
                        for u, buf in enumerate((cout, gbuf)):
                            sp.dma_start(buf[:], one(conv_d, 2 * j + u)).then_inc(cdev_loaded, 16)
                    if idx < 5:
                        sp.wait_ge(y_split, 4 * (idx + 1) + j)
                        load_branch(idx + 1, j)

            shift = 24
            for n in (N_MIX, N_MIX + KB, N_Q, N_Q + KB):
                shift += KB if n in (N_MIX + KB, N_Q + KB) else 0
                weight_tiles(n, n + KB, shift)
            sp.wait_ge(mm_done, N_Q + KB)
            for q, buf in enumerate((kh, kl, vh, vl)):
                sp.dma_start(buf[:].bitcast(F32).rearrange("p a b -> p (a b)"), kv_d[q]).then_inc(kv_loaded, 16)
            weight_tiles(N_WO, N_WO + KB, shift)
            weight_tiles(N_WO + KB, N_MLP, shift + KB)
            shift += KB
            weight_tiles(N_MLP, N_MLP + 2 * FFB * KB, shift)
            weight_tiles(N_MLP + 2 * FFB * KB, N_END, shift + 2 * FFB * KB)
            sp.wait_ge(out_stored, 16 * 8)


def kernel(x, mem, hgrn_lower_bounds, norm_pre_mix, norm_post_mix, w_in, lru_conv_w, lru_conv_b, lru_wx, lru_bx,
           lru_wa, lru_ba, lru_lambda, hgrn_norm_g, conf_dw_w, conf_dw_b, conf_ln_g, conf_ln_b, w_branch, w_mix_out,
           norm_pre_xa, norm_post_xa, mem_norm_g, xa_wq, xa_wkv, xa_wo, norm_pre_mlp, norm_post_mlp, mlp_w1, mlp_w2):
    import numpy as np
    import concourse.bacc as bacc
    from concourse.bass_utils import run_bass_kernel_spmd

    f32 = np.float32

    def tiles(w):
        w = np.asarray(w, f32)
        return w.reshape(KB, P, -1, P).transpose(2, 1, 0, 3).reshape(-1, P, KB * P)

    win = tiles(np.asarray(w_in)[0]).reshape(-1, KB, P, KB * P)
    lx, ly, hq, hf, hi, hgate, ca, cg = (win[i] for i in range(8))
    wall = [tiles(np.asarray(xa_wkv)[0])]
    for c in range(KB):
        wall += [ca[c:c + 1], cg[c:c + 1]]
    for b in range(KB // 2):
        wall += [lx[2 * b:2 * b + 2], ly[2 * b:2 * b + 2]]
    for h in range(KB):
        wall += [w[h:h + 1] for w in (hf, hq, hi, hgate)]
    wall += [win[8 + i] for i in range(3)]
    wall += [tiles(np.asarray(w_branch)[0, i]) for i in range(3)]
    wall += [tiles(np.asarray(w)[0]) for w in (w_mix_out, xa_wq, xa_wo)]
    w1, w2 = np.asarray(mlp_w1)[0], np.asarray(mlp_w2)[0]
    for kind, b in MLP_ORDER:
        block = slice(b * D, (b + 1) * D)
        wall.append(tiles(w1[:, block] if kind == "up" else w2[block]))
    wall = np.concatenate(wall)

    gates = np.stack([np.asarray(lru_wx)[0], np.asarray(lru_wa)[0]], 1)
    gates = gates.reshape(4, 2, 2, P, 2 * P).transpose(0, 3, 1, 2, 4).reshape(4, P, 8 * P)

    params = np.empty((P, KB, NP), f32)
    for j, v in ((G_PRE_MIX, norm_pre_mix), (G_POST_MIX, norm_post_mix), (G_PRE_XA, norm_pre_xa),
                 (G_POST_XA, norm_post_xa), (G_PRE_MLP, norm_pre_mlp), (G_POST_MLP, norm_post_mlp),
                 (G_MEM, mem_norm_g), (HLB, hgrn_lower_bounds), (LRU_B, lru_conv_b), (LRU_BX, lru_bx),
                 (LRU_BA, lru_ba), (LRU_LAM, lru_lambda), (CONF_B, conf_dw_b), (CONF_G, conf_ln_g),
                 (CONF_LB, conf_ln_b)):
        params[:, :, j] = np.asarray(v)[0].reshape(KB, P).T
    params[:, :, HG_G] = np.asarray(hgrn_norm_g)[0][:, None]
    params[:, :, LRU_W:CONF_W] = np.asarray(lru_conv_w)[0].reshape(LW, KB, P).transpose(2, 1, 0)
    params[:, :, CONF_W:] = np.asarray(conf_dw_w)[0].reshape(CW, KB, P).transpose(2, 1, 0)

    j, r = np.arange(CHUNK)[:, None], np.arange(CHUNK // 2)[None]
    masks = np.stack([(j // (2 * c) == r // c) & (j % (2 * c) < c) for c in (2 ** l for l in range(LEVELS))], 1).astype(f32)

    arrays = dict(xT=np.ascontiguousarray(np.asarray(x)[0].T), memT=np.ascontiguousarray(np.asarray(mem)[0].T),
                  wall=np.ascontiguousarray(wall), lru_gates=np.ascontiguousarray(gates), params=params,
                  masks=np.ascontiguousarray(masks), ident_in=np.eye(P, dtype=f32))
    nc = bacc.Bacc("TRN2", target_bir_lowering=False, num_devices=1)
    handles = {k: nc.dram_tensor(k, list(a.shape), F32, kind="ExternalInput").ap()
               for k, a in arrays.items()}
    out = nc.dram_tensor("out", [D, T], F32, kind="ExternalOutput").ap()
    build(nc, *handles.values(), out)
    res = run_bass_kernel_spmd(nc, [arrays], core_ids=[0])
    return np.ascontiguousarray(res.results[0]["out"].T)[None]
```
